# Optimizing a Trainium2 kernel written in Bass

```python
import math
import jax
import jax.numpy as jnp
from jax import lax
import numpy as np

D_MODEL = 1024
BATCH = 1
SEQ = 256
DEPTH = 2
DEC_BATCH = 1
DEC_SEQ = 256
PAST_LEN = 128

GLA_HEADS = 4
GLA_DK = 64
GLA_DV = 128
GLA_KW = GLA_HEADS * GLA_DK
GLA_WIDTH = GLA_HEADS * GLA_DV
GLA_GATE_RANK = 16
GLA_GATE_TEMP = 16.0
GLA_CHUNK = 64

HY_WIDTH = D_MODEL - GLA_WIDTH
HY_ORDER = 2
HY_DIRS = 2
HY_SHORT = 3
HY_BANDS = 8
HY_EMB = 1 + 2 * HY_BANDS
HY_FFN = 64
HY_N_FILT = HY_ORDER * HY_DIRS * HY_WIDTH
HY_FAST_DECAY = 0.3
HY_SLOW_DECAY = 1.5
HY_DECAY_TARGET = 1e-2

D_FF = -(-8 * D_MODEL // (3 * 256)) * 256
NORM_EPS = 1e-6

IN_SIZES = (GLA_KW, GLA_KW, GLA_WIDTH, GLA_WIDTH, 2 * GLA_GATE_RANK, (HY_ORDER + 1) * HY_WIDTH)
IN_WIDTH = sum(IN_SIZES)

kernel_name = "hybrid_gla_hyena_encoder"

def rmsnorm(x, w):
    xf = x.astype(jnp.float32)
    y = xf * lax.rsqrt(jnp.mean(xf * xf, axis=-1, keepdims=True) + NORM_EPS)
    return (y * w.astype(jnp.float32)).astype(x.dtype)

def gla_chunk_scan(q, k, v, g):
    B, H, T, DK = q.shape
    DV = v.shape[-1]
    C = GLA_CHUNK
    NC = T // C

    def chunks(a):
        return jnp.moveaxis(a.reshape(B, H, NC, C, a.shape[-1]), 2, 0)

    qc, kc, vc, gc = chunks(q), chunks(k), chunks(v), chunks(g)
    bc = jnp.cumsum(gc, axis=-2)
    lower = jnp.tril(jnp.ones((C, C), dtype=bool))[:, :, None]

    def step(S, inp):
        qi, ki, vi, bi = inp
        o_inter = jnp.einsum('bhik,bhkv->bhiv', qi * jnp.exp(bi), S)
        diff = jnp.where(lower, bi[:, :, :, None, :] - bi[:, :, None, :, :], -jnp.inf)
        A = jnp.einsum('bhik,bhjk,bhijk->bhij', qi, ki, jnp.exp(diff))
        o = o_inter + jnp.einsum('bhij,bhjv->bhiv', A, vi)
        b_last = bi[:, :, -1:, :]
        S = jnp.exp(b_last[:, :, 0, :, None]) * S + jnp.einsum(
            'bhjk,bhjv->bhkv', ki * jnp.exp(b_last - bi), vi)
        return S, o

    S0 = jnp.zeros((B, H, DK, DV), jnp.float32)
    _, o = lax.scan(step, S0, (qc, kc, vc, bc))
    return jnp.moveaxis(o, 0, 2).reshape(B, H, T, DV)

def gla_group(q, k, v, r, g_lr, wg_f, bg_f, wg_b, bg_b, norm_w):
    B, T, _ = q.shape

    def heads(a, d):
        return a.reshape(B, T, GLA_HEADS, d).transpose(0, 2, 1, 3).astype(jnp.float32)

    qh = heads(q, GLA_DK) * (GLA_DK ** -0.5)
    kh = heads(k, GLA_DK)
    vh = heads(v, GLA_DV)
    lr_f, lr_b = jnp.split(g_lr, 2, axis=-1)

    def log_gate(z, w, b):
        return jax.nn.log_sigmoid(heads(z @ w + b, GLA_DK)) / GLA_GATE_TEMP

    g_f = log_gate(lr_f, wg_f, bg_f)
    g_b = log_gate(lr_b, wg_b, bg_b)
    rev = lambda a: jnp.flip(a, axis=2)
    o = gla_chunk_scan(qh, kh, vh, g_f) + rev(gla_chunk_scan(rev(qh), rev(kh), rev(vh), rev(g_b)))
    o = rmsnorm(o.transpose(0, 2, 1, 3), norm_w)
    return o.reshape(B, T, GLA_WIDTH).astype(r.dtype) * jax.nn.silu(r)

def short_conv_centred(u, w, b):
    T = u.shape[1]
    up = jnp.pad(u, ((0, 0), (1, 1), (0, 0)))
    return up[:, :T] * w[0] + up[:, 1:T + 1] * w[1] + up[:, 2:] * w[2] + b

def hyena_filters(L, w1, b1, freq1, w2, b2, freq2, w3):
    t = jnp.linspace(0.0, 1.0, L, dtype=jnp.float32)[:, None]
    pos_w = (2.0 * math.pi / L) * jnp.arange(L, dtype=jnp.float32)[:, None]
    bands = jnp.linspace(1e-4, HY_BANDS - 1.0, HY_BANDS, dtype=jnp.float32)
    feats = jnp.concatenate([t, jnp.cos(bands * pos_w), -jnp.sin(bands * pos_w)], axis=-1)
    feats = feats.astype(w1.dtype)
    hid = jnp.sin(freq1 * (feats @ w1 + b1))
    hid = jnp.sin(freq2 * (hid @ w2 + b2))
    filt = (hid @ w3).astype(jnp.float32).reshape(L, HY_ORDER, HY_DIRS, HY_WIDTH)
    max_decay = math.log(HY_DECAY_TARGET) / HY_FAST_DECAY
    min_decay = math.log(HY_DECAY_TARGET) / HY_SLOW_DECAY
    deltas = jnp.abs(jnp.linspace(min_decay, max_decay, HY_WIDTH, dtype=jnp.float32))
    filt = filt * jnp.exp(-t * deltas)[:, None, None, :]
    fwd, bwd = filt[:, :, 0], filt[:, :, 1]
    kern = jnp.concatenate([fwd, jnp.zeros_like(fwd[:1]), jnp.flip(bwd[1:], axis=0)], axis=0)
    return jnp.fft.rfft(kern, axis=0)

def fft_long_conv(u, k_freq, d):
    L = u.shape[1]
    uf = u.astype(jnp.float32)
    y = jnp.fft.irfft(jnp.fft.rfft(uf, n=2 * L, axis=1) * k_freq, n=2 * L, axis=1)[:, :L]
    return (y + uf * d.astype(jnp.float32)).astype(u.dtype)

def hyena_group(u, conv_w, conv_b, w1, b1, freq1, w2, b2, freq2, w3, skip, norm_w):
    u = short_conv_centred(u, conv_w, conv_b)
    v, x1, x2 = jnp.split(u, HY_ORDER + 1, axis=-1)
    k_freq = hyena_filters(u.shape[1], w1, b1, freq1, w2, b2, freq2, w3)
    z = x1 * fft_long_conv(v, k_freq[:, 0], skip[0])
    z = x2 * fft_long_conv(z, k_freq[:, 1], skip[1])
    return rmsnorm(z, norm_w)

def encoder_layer(x, norm_mix, w_in, gla_wg_f, gla_bg_f, gla_wg_b, gla_bg_b, gla_norm,
                  hy_conv_w, hy_conv_b, hy_w1, hy_b1, hy_freq1, hy_w2, hy_b2, hy_freq2, hy_w3,
                  hy_skip, hy_norm, w_out, norm_ffn, w_gate, w_up, w_down):
    h = rmsnorm(x, norm_mix)
    proj = jnp.einsum('btd,de->bte', h, w_in)
    q, k, v, r, g_lr, hy_in = jnp.split(proj, np.cumsum(IN_SIZES)[:-1].tolist(), axis=-1)
    o_gla = gla_group(q, k, v, r, g_lr, gla_wg_f, gla_bg_f, gla_wg_b, gla_bg_b, gla_norm)
    o_hy = hyena_group(hy_in, hy_conv_w, hy_conv_b, hy_w1, hy_b1, hy_freq1, hy_w2, hy_b2,
                       hy_freq2, hy_w3, hy_skip, hy_norm)
    x = x + jnp.einsum('bte,ed->btd', jnp.concatenate([o_gla, o_hy], axis=-1), w_out)
    h = rmsnorm(x, norm_ffn)
    ff = jax.nn.silu(h @ w_gate) * (h @ w_up)
    return x + ff @ w_down

def encoder_trunk(x, weights, norm_final):
    for layer in range(DEPTH):
        x = encoder_layer(x, *[w[layer] for w in weights])
    return rmsnorm(x, norm_final)

def setup_inputs(seed: int = 0) -> dict:
    key = jax.random.key(seed)
    keys = jax.random.split(key, 26)

    def nrm(i, shape, scale):
        return scale * jax.random.normal(keys[i], shape, jnp.float32)

    L = DEPTH
    return {
        'x_prompt': nrm(0, (BATCH, SEQ, D_MODEL), 1.0),
        'x_sample': nrm(1, (DEC_BATCH, DEC_SEQ, D_MODEL), 1.0),
        'norm_mix': 1.0 + nrm(2, (L, D_MODEL), 0.02),
        'w_in': nrm(3, (L, D_MODEL, IN_WIDTH), D_MODEL ** -0.5),
        'gla_wg_f': nrm(4, (L, GLA_GATE_RANK, GLA_KW), GLA_GATE_RANK ** -0.5),
        'gla_bg_f': nrm(5, (L, GLA_KW), 0.1),
        'gla_wg_b': nrm(6, (L, GLA_GATE_RANK, GLA_KW), GLA_GATE_RANK ** -0.5),
        'gla_bg_b': nrm(7, (L, GLA_KW), 0.1),
        'gla_norm': 1.0 + nrm(8, (L, GLA_DV), 0.02),
        'hy_conv_w': nrm(9, (L, HY_SHORT, (HY_ORDER + 1) * HY_WIDTH), 0.5),
        'hy_conv_b': nrm(10, (L, (HY_ORDER + 1) * HY_WIDTH), 0.02),
        'hy_w1': nrm(11, (L, HY_EMB, HY_FFN), HY_EMB ** -0.5),
        'hy_b1': nrm(12, (L, HY_FFN), 0.1),
        'hy_freq1': 1.0 + nrm(13, (L, HY_FFN), 0.02),
        'hy_w2': nrm(14, (L, HY_FFN, HY_FFN), HY_FFN ** -0.5),
        'hy_b2': nrm(15, (L, HY_FFN), 0.1),
        'hy_freq2': 1.0 + nrm(16, (L, HY_FFN), 0.02),
        'hy_w3': nrm(17, (L, HY_FFN, HY_N_FILT), 0.01),
        'hy_skip': nrm(18, (L, HY_ORDER, HY_WIDTH), 0.1),
        'hy_norm': 1.0 + nrm(19, (L, HY_WIDTH), 0.02),
        'w_out': nrm(20, (L, D_MODEL, D_MODEL), D_MODEL ** -0.5),
        'norm_ffn': 1.0 + nrm(21, (L, D_MODEL), 0.02),
        'w_gate': nrm(22, (L, D_MODEL, D_FF), D_MODEL ** -0.5),
        'w_up': nrm(23, (L, D_MODEL, D_FF), D_MODEL ** -0.5),
        'w_down': nrm(24, (L, D_FF, D_MODEL), D_FF ** -0.5),
        'norm_final': 1.0 + nrm(25, (D_MODEL,), 0.02),
    }

def reference(x_prompt, x_sample, norm_mix, w_in, gla_wg_f, gla_bg_f, gla_wg_b, gla_bg_b,
              gla_norm, hy_conv_w, hy_conv_b, hy_w1, hy_b1, hy_freq1, hy_w2, hy_b2, hy_freq2,
              hy_w3, hy_skip, hy_norm, w_out, norm_ffn, w_gate, w_up, w_down, norm_final):
    weights = (norm_mix, w_in, gla_wg_f, gla_bg_f, gla_wg_b, gla_bg_b, gla_norm,
               hy_conv_w, hy_conv_b, hy_w1, hy_b1, hy_freq1, hy_w2, hy_b2, hy_freq2, hy_w3,
               hy_skip, hy_norm, w_out, norm_ffn, w_gate, w_up, w_down)
    y_prompt = encoder_trunk(x_prompt, weights, norm_final)
    y_sample = encoder_trunk(x_sample, weights, norm_final)
    return (y_prompt, y_sample)


_drawn_inputs = setup_inputs


def setup_inputs(seed=0):
    import zlib

    import numpy as np

    out = dict(_drawn_inputs(seed))
    spreads = {}
    factors = {'gla_bg_f': 3.488,
     'gla_bg_b': 3.5,
     'gla_norm': 5.228,
     'hy_freq1': 3.156,
     'hy_freq2': 2.682,
     'hy_norm': 2.991,
     'norm_ffn': 2.913,
     'norm_final': 2.812}
    for name, (base, spread) in spreads.items():
        noise = np.random.default_rng([zlib.crc32(name.encode()), seed]).standard_normal(out[name].shape)
        drawn = base * np.exp(spread * noise) if base else spread * noise
        out[name] = jnp.asarray(drawn.astype(out[name].dtype))
    for name, factor in factors.items():
        out[name] = (out[name] * factor).astype(out[name].dtype)
    return out
```

```python
import math
from contextlib import ExitStack

import numpy as np

import concourse.bass as bass
from concourse import mybir

F32 = mybir.dt.float32
F32R = mybir.dt.float32r
U8 = mybir.dt.uint8
ALU = mybir.AluOpType
ACT = mybir.ActivationFunctionType

P = 128
D_MODEL, SEQ, NSEQ, DEPTH = 1024, 256, 2, 2
TOK = SEQ * NSEQ
HEADS, DK, DV, RANK, TEMP = 4, 64, 128, 16, 16.0
HY, ORDERS = 512, 2
EMB, FFN_HY = 17, 64
D_FF = 2816
EPS = 1e-6
KT = D_MODEL // P
FT = D_FF // P
CT = HY // P
TT = TOK // P

U_Q, U_K, U_V, U_HV, U_X1, U_X2, U_R = 0, 2, 4, 8, 12, 16, 20
U_OUT = 24
U_FFN = U_OUT + KT
U_DOWN = U_FFN + 2 * FT
UNITS = U_DOWN + FT
RING = 2

LEVELS = (128, 64, 32, 16, 8, 4, 2, 1)
MASKED = (16, 8, 4, 2, 1)

C_GLR = 0
C_NMIX = C_GLR + KT * 2 * RANK
C_NFFN = C_NMIX + KT
C_CW = C_NFFN + KT
C_CB = C_CW + 3 * 12
C_GN = C_CB + 12
C_BG = C_GN + 1
C_HN = C_BG + HEADS
C_B1 = C_HN + CT
C_F1 = C_B1 + 1
C_B2 = C_F1 + 1
C_F2 = C_B2 + 1
C_MISC = C_F2 + 1
C_W1 = C_MISC + HEADS * P
C_W2 = C_W1 + FFN_HY
C_W3 = C_MISC + ORDERS * HY
N_PAR = C_W3 + ORDERS * HY
SKIP_ROW = 64

K_ID = 0
K_FEAT = K_ID + P + P // 2
K_DFT = K_FEAT + SEQ
K_INV = K_DFT + 6 * 2 * P
K_WIN = K_INV + 4 * SEQ
N_CST = K_WIN + 2 * HY
DFT_C0, DFT_C1, DFT_C0N, DFT_S0, DFT_S0N, DFT_S1 = range(6)


class Signal:

    def __init__(self, sem, per_layer, credit=0):
        self.sem, self.per_layer, self.credit = sem, per_layer, credit

    def at(self, L, n):
        return L * self.per_layer + (n + self.credit)


class Steps:

    def __init__(self, sem, per_layer):
        self.sem, self.per_layer, self.n = sem, per_layer, 0

    def next(self, L):
        self.n += 1
        return L * self.per_layer + self.n


def build(nc, x_d, units_d, par_d, cst_d, mask_d, fin_d, y_d):
    with ExitStack() as ctx:
        base = (nc.sbuf_base + 63) // 64 * 64
        place = [base]

        def sb(name, cols, dt=F32, at=None):
            size = cols * (1 if dt == U8 else 4)
            off = at
            if at is None:
                off = place[0]
                place[0] += (size + 31) // 32 * 32
            return nc.alloc_sbuf_tensor_at(name, [P, cols], dt, offset=off)

        def sem(name):
            return ctx.enter_context(nc.semaphore(name))

        x_t = sb("x", KT * TOK)
        x = x_t[:, :].rearrange("p (k t) -> p k t", k=KT)
        h_hi = sb("h_hi", KT * TOK, F32R)[:, :].rearrange("p (k t) -> p k t", k=KT)
        h_lo = sb("h_lo", KT * TOK, F32R)[:, :].rearrange("p (k t) -> p k t", k=KT)
        w_raw = sb("w_raw", RING * 1024)[:, :].rearrange("p (r b c) -> p r b c", r=RING, b=8)
        w_hi = sb("w_hi", RING * 1024, F32R)[:, :].rearrange("p (r b c) -> p r b c", r=RING, b=8)
        w_lo = sb("w_lo", RING * 1024, F32R)[:, :].rearrange("p (r b c) -> p r b c", r=RING, b=8)
        cst = sb("cst", N_CST)
        mask = sb("mask", 2 * len(MASKED) * P, U8)[:, :].rearrange("p (l d c) -> p l d c", l=len(MASKED), d=2)
        par = sb("par", N_PAR)
        fin = sb("fin", KT)
        glr_t = sb("glr_t", TOK)
        ones = sb("ones", P)
        sq = sb("sq", 2 * TOK)[:, :].rearrange("p (r t) -> p r t", r=2)
        nrm = sb("nrm", 2 * TOK)[:, :].rearrange("p (r t) -> p r t", r=2)
        rstd = sb("rstd", TOK)
        carrier = sb("carrier", 8)
        sg_at = place[0]
        sg = sb("sg", 2 * TOK + SEQ)[:, 0:2 * TOK].rearrange("p (r t) -> p r t", r=2)
        arg = sb("arg", SEQ, at=sg_at)
        turn = sb("turn", SEQ, at=sg_at + 4 * SEQ)
        hid1 = sb("hid1", SEQ, at=sg_at + 8 * SEQ)
        hid_a = sb("hid_a", SEQ, at=sg_at + 12 * SEQ)
        hid_b = sb("hid_b", SEQ, at=sg_at + 16 * SEQ)
        mix = place[0]
        g1 = sb("g1", HEADS * TOK)[:, :].rearrange("p (h t) -> p h t", h=HEADS)
        g2 = sb("g2", HEADS * TOK)[:, :].rearrange("p (h t) -> p h t", h=HEADS)
        pre_t = sb("pre", HEADS * NSEQ * (SEQ + 1))
        pre = pre_t[:, :].rearrange("p (h s t) -> p h s t", h=HEADS, s=NSEQ)
        bt = sb("bt", HEADS * TOK)[:, :].rearrange("p (h t) -> p h t", h=HEADS)
        dd = sb("dd", 4 * TOK)[:, :].rearrange("p (r t) -> p r t", r=4)
        xx = sb("xx", 4 * TOK)[:, :].rearrange("p (r t) -> p r t", r=4)
        amat = sb("amat", 4 * SEQ)[:, :].rearrange("p (k s j i) -> p k s j i", k=2, s=NSEQ, j=2)
        glr_hi = sb("glr_hi", KT * P, F32R, at=place[0])[:, :].rearrange("p (k r c) -> p k r c", k=KT, r=4)
        glr_lo = sb("glr_lo", KT * P, F32R, at=place[0] + 4 * KT * P)[:, :]\
            .rearrange("p (k r c) -> p k r c", k=KT, r=4)
        v_tok = sb("v_tok", HEADS * TOK)[:, :].rearrange("p (h t c) -> p h t c", h=HEADS, t=TT)
        u = sb("u", 12 * TOK)[:, :].rearrange("p (c t) -> p c t", c=12)
        kf = sb("kf", ORDERS * 5 * HY)[:, :].rearrange("p (o f c) -> p o f c", o=ORDERS, f=5)
        hid_hi = sb("hid_hi", FT * TOK, F32R, at=mix)[:, :].rearrange("p (f t) -> p f t", f=FT)
        hid_lo = sb("hid_lo", FT * TOK, F32R, at=mix + 4 * FT * TOK)[:, :].rearrange("p (f t) -> p f t", f=FT)
        assert place[0] <= nc.sbuf_usable_end
        assert mix + 8 * FT * TOK <= place[0]
        o_t, r_t = g1, bt
        mask_f = xx.rearrange("p r t -> p (r t)")[:, 0:2 * len(MASKED) * P]
        ab = dd.rearrange("p (t k) c -> p t k c", t=2)
        u_tok = dd
        spec = (g2, xx)
        prod = pre_t[:, 0:4 * HY].rearrange("p (r c) -> p r c", r=4)
        o_rstd = v_tok.rearrange("p h t c -> p h (t c)")
        u_seq = u.rearrange("p c (s t) -> p c s t", s=NSEQ)
        ident = cst[:, K_ID:K_ID + P]
        feat = cst[0:EMB, K_FEAT:K_FEAT + SEQ]
        glr_w = par[:, C_GLR:C_NMIX].rearrange("p (k c) -> p k c", k=KT)
        skip_sel = cst[:, K_ID + SKIP_ROW:K_ID + SKIP_ROW + P]
        dft = cst[:, K_DFT:K_INV].rearrange("p (f k c) -> p f k c", f=6, k=2)
        inv = cst[:, K_INV:K_WIN].rearrange("p (f t) -> p f t", f=4)
        win = cst[:, K_WIN:N_CST].rearrange("p (t c) -> p t c", t=2)

        ps = ctx.enter_context(nc.psum_tensor("ps", [P, 8, TOK], F32))

        s_x, s_cst = sem("s_x"), sem("s_cst")
        s_ones, s_pre0 = sem("s_ones"), sem("s_pre0")
        s_y = sem("s_y")
        raw = [Signal(sem(f"s_raw{j}"), 16 * UNITS // RING) for j in range(RING)]
        parl = Signal(sem("s_par"), 16)
        hi = Signal(sem("s_hi"), UNITS)
        lo = Signal(sem("s_lo"), UNITS, RING)
        unit = Signal(sem("s_unit"), UNITS, RING)
        res = Signal(sem("s_res"), 2 * KT, 1)
        sqd = Signal(sem("s_sqd"), 24)
        stat = Signal(sem("s_stat"), 24, 2)
        inv_ms = Signal(sem("s_inv_ms"), 7)
        o_ms = Signal(sem("s_o_ms"), 4)
        rms = Signal(sem("s_rms"), 7)
        normed = Signal(sem("s_normed"), 24, 1)
        ahi = Signal(sem("s_ahi"), 24)
        alo = Signal(sem("s_alo"), 24, 2)
        glrw = Signal(sem("s_glrw"), 2)
        glrw2 = Signal(sem("s_glrw2"), 1)
        glrp = Signal(sem("s_glrp"), 1)
        glrt = Signal(sem("s_glrt"), 1)
        net = Signal(sem("s_net"), 2)
        turned = Signal(sem("s_turned"), 2)
        sine = Signal(sem("s_sine"), 2)
        hidab = Signal(sem("s_hidab"), 1)
        abp = Signal(sem("s_abp"), 8)
        abw = Signal(sem("s_abw"), 8)
        kfp = Signal(sem("s_kfp"), 10)
        kfc = Signal(sem("s_kfc"), 10)
        zp = Signal(sem("s_zp"), 4)
        zabs = Signal(sem("s_zabs"), 4)
        zln = Signal(sem("s_zln"), 4)
        zmin = Signal(sem("s_zmin"), 4)
        scan = Signal(sem("s_scan"), 4)
        btd = Signal(sem("s_btd"), 4)
        evac = Signal(sem("s_evac"), 12)
        mid = Signal(sem("s_mid"), 12)
        conv = Signal(sem("s_conv"), 12)
        expo = Signal(sem("s_expo"), 32)
        fact = Signal(sem("s_fact"), 32)
        xld = Signal(sem("s_xld"), 32)
        pair = Signal(sem("s_pair"), 16)
        big = Signal(sem("s_big"), 4)
        put = Signal(sem("s_put"), 40)
        vtp = Signal(sem("s_vtp"), 4)
        vtc = Signal(sem("s_vtc"), 4)
        op_ = Signal(sem("s_op"), 4)
        oc = Signal(sem("s_oc"), 4)
        silu_r = Signal(sem("s_silu_r"), 1)
        utp = Signal(sem("s_utp"), 8)
        utc = Signal(sem("s_utc"), 8)
        ufp = Signal(sem("s_ufp"), 16)
        prd = Signal(sem("s_prd"), 8)
        yfd = Signal(sem("s_yfd"), 8)
        invp = Signal(sem("s_invp"), 8)
        gated = Signal(sem("s_gated"), 8)
        gate = Signal(sem("s_gate"), FT, 2)
        hidn = Signal(sem("s_hidn"), FT, 2)
        hhi = Signal(sem("s_hhi"), FT)
        hlo = Signal(sem("s_hlo"), FT, 2)
        down = Signal(sem("s_down"), KT)
        dve = Steps(sem("s_dve"), 33)
        acs = Steps(sem("s_acs"), 8)

        def lvl(h, l):
            return h * len(LEVELS) + l

        def first(h):
            return 5 + 5 * h

        def head_pair(slot):
            h, p = divmod(slot - first(0), 5)
            return (h, p) if 0 <= h < HEADS and p < 4 else None

        block = ctx.enter_context(nc.Block())

        @block.sync
        def _(sp):
            sp.dma_start(x_t[:, :], x_d).then_inc(s_x, 16)
            sp.dma_start(cst[:, :], cst_d).then_inc(s_cst, 16)
            sp.dma_start(mask_f, mask_d).then_inc(s_cst, 16)
            sp.dma_start(fin[:, :], fin_d).then_inc(s_cst, 16)
            with sp.Fori(0, DEPTH) as L:
                sp.wait_ge(normed.sem, normed.at(L, 0))
                sp.dma_start(par[:, :], par_d[L]).then_inc(parl.sem, 16)
                with sp.Fori(0, UNITS // RING) as i:
                    for j in range(RING):
                        sp.wait_ge(lo.sem, L * UNITS + i * RING + (j + 1))
                        sp.dma_start(w_raw[:, j], units_d[L * UNITS + i * RING + j]).then_inc(raw[j].sem, 16)
            for kt in range(KT):
                sp.wait_ge(normed.sem, normed.at(DEPTH, kt + 1))
                sp.dma_start(y_d[:, kt, :], x[:, kt, :]).then_inc(s_y, 16)
            sp.wait_ge(s_y, 16 * KT)

        @block.scalar
        def _(act):
            def hi_unit(L, n, j, i=None, per=0):
                at = n if i is None else i * per + n
                act.wait_ge(raw[j].sem, L * raw[j].per_layer + (n // RING + 1) * 16 if i is None
                            else L * raw[j].per_layer + i * (per // RING * 16) + (n // RING + 1) * 16)
                act.wait_ge(unit.sem, L * UNITS + at + 1)
                nc.scalar.activation(w_hi[:, j], w_raw[:, j], ACT.Copy).then_inc(hi.sem, 1)

            def square(L, n, src):
                act.wait_ge(stat.sem, stat.at(L, n - 1))
                nc.scalar.activation(sq[:, n % 2], src, ACT.Square).then_inc(sqd.sem, 1)

            def root(L, n, t):
                act.wait_ge(inv_ms.sem, inv_ms.at(L, n + 1))
                nc.scalar.activation(t, t, ACT.Sqrt).then_inc(rms.sem, 1)

            def round_tile(L, n, kt, src):
                act.wait_ge(normed.sem, normed.at(L, n + 1))
                nc.scalar.activation(h_hi[:, kt], src, ACT.Copy).then_inc(ahi.sem, 1)

            def sine_of(L, n, dst, rows):
                act.wait_ge(turned.sem, turned.at(L, n + 1))
                nc.scalar.activation(dst[0:rows, :], arg[0:rows, :], ACT.Sin).then_inc(sine.sem, 1)

            def filter_copy(L, o):
                for f in range(5):
                    act.wait_ge(kfp.sem, kfp.at(L, 5 * o + f + 1))
                    nc.scalar.activation(kf[:, o, f], ps[:, 2 + f, :], ACT.Copy).then_inc(kfc.sem, 1)

            def gates(L):
                act.wait_ge(kfp.sem, kfp.at(L, 10))
                for h in range(HEADS):
                    act.wait_ge(zp.sem, zp.at(L, h + 1))
                    nc.scalar.activation(dd[:, h], ps[:, 2 + h, :], ACT.Abs,
                                         bias=par[:, C_BG + h:C_BG + h + 1]).then_inc(zabs.sem, 1)
                for h in range(HEADS):
                    act.wait_ge(zabs.sem, zabs.at(L, h + 1))
                    a = acs.next(L)
                    nc.scalar.activation(dd[:, h], dd[:, h], ACT.Exp, scale=-1.0).then_inc(acs.sem, 1)
                for h in range(HEADS):
                    act.wait_ge(acs.sem, a - (HEADS - 1 - h))
                    nc.scalar.activation(dd[:, h], dd[:, h], ACT.Ln, bias=1.0).then_inc(zln.sem, 1)

            def evacuate(L, t):
                b = ps[:, t % 2, :]
                act.wait_ge(unit.sem, unit.at(L, t + 1))
                if t < U_V:
                    scale, fwd, bwd = (DK ** -0.5, g2, g1) if t < U_K else (1.0, g1, g2)
                    for n in range(2):
                        h = 2 * (t % 2) + n
                        rows = slice(DK * n, DK * n + DK)
                        nc.scalar.activation(fwd[0:DK, h], b[rows], ACT.Copy, scale=scale)
                        last = nc.scalar.activation(bwd[DK:P, h], b[rows], ACT.Copy, scale=scale)
                    last.then_inc(evac.sem, 1)
                elif t < U_HV:
                    nc.scalar.activation(u[:, 8 + t - U_V], b, ACT.Copy).then_inc(evac.sem, 1)
                elif t < U_R:
                    c = t - U_HV
                    if t >= U_X2:
                        act.wait_ge(vtp.sem, vtp.at(L, HEADS))
                    nc.scalar.activation(u[:, c], b, ACT.Identity, bias=par[:, C_CB + c:C_CB + c + 1],
                                         scale=par[:, C_CW + 12 + c:C_CW + 13 + c]).then_inc(mid.sem, 1)
                else:
                    h = t - U_R
                    act.wait_ge(expo.sem, expo.at(L, 8 * (h + 1)))
                    nc.scalar.activation(r_t[:, h], b, ACT.Copy).then_inc(evac.sem, 1)

            def factors(L, slot):
                hp = head_pair(slot + 1)
                if hp:
                    for l in (2 * hp[1], 2 * hp[1] + 1):
                        n = lvl(hp[0], l)
                        act.wait_ge(expo.sem, expo.at(L, n + 1))
                        nc.scalar.activation(dd[:, n % 4], dd[:, n % 4], ACT.Exp,
                                             scale=1.0 / TEMP).then_inc(fact.sem, 1)

            def big_levels(L, h):
                act.wait_ge(pair.sem, pair.at(L, 4 * h + 2))
                if h:
                    act.wait_ge(op_.sem, op_.at(L, h))
                fw = ps[:, 6:8, :].rearrange("p s (k j i) -> p s k j i", k=2, j=2)
                bw = ps[:, 2:4, :].rearrange("p s (k j i) -> p s k j i", k=2, j=2)
                a = acs.next(L)
                nc.scalar.activation(amat[:, 0], fw[:, :, 0], ACT.Copy)
                nc.scalar.activation(amat[:, 1, :, 0], fw[:, :, 1, 0], ACT.Copy)
                nc.scalar.activation(amat[:, 1, :, 1], bw[:, :, 1, 1], ACT.Copy).then_inc(acs.sem, 1)
                act.wait_ge(acs.sem, a)
                for rows, cols in ((slice(64, P), slice(0, 64)), (slice(32, 64), slice(0, 32)),
                                   (slice(96, P), slice(64, 96))):
                    last = nc.scalar.activation(amat[rows, 0, :, :, cols], bw[rows, :, 0, :, cols], ACT.Copy)
                last.then_inc(big.sem, 1)

            def v_copy(L, h):
                act.wait_ge(vtp.sem, vtp.at(L, h + 1))
                nc.scalar.activation(v_tok[:, h].rearrange("p t c -> p (t c)"), ps[:, 6 + h % 2, :],
                                     ACT.Copy).then_inc(vtc.sem, 1)

            def before(L, slot):
                for h in range(HEADS):
                    if slot == first(h) + 3:
                        big_levels(L, h)
                    if slot == first(h) + 6:
                        act.wait_ge(op_.sem, op_.at(L, h + 1))
                        nc.scalar.activation(o_t[:, h], ps[:, 2, :], ACT.Copy).then_inc(oc.sem, 1)
                if slot == 9:
                    v_copy(L, 0)
                    v_copy(L, 1)
                if slot == 10:
                    v_copy(L, 2)
                    v_copy(L, 3)
                factors(L, slot)

            def after(L, slot):
                if slot == 0:
                    act.wait_ge(glrp.sem, glrp.at(L, 1))
                    nc.scalar.activation(glr_t[0:2 * RANK, :], ps[0:2 * RANK, 6, :], ACT.Copy)\
                        .then_inc(glrt.sem, 1)
                if slot < 2:
                    filter_copy(L, slot)
                if slot == 2:
                    gates(L)

            def turn_copy(L, o):
                for t in range(TT):
                    act.wait_ge(utp.sem, utp.at(L, 4 * o + t + 1))
                    nc.scalar.activation(u_tok[:, t], ps[:, (0, 1, 6, 7)[t], :], ACT.Copy)\
                        .then_inc(utc.sem, 1)

            act.sem_inc(gate.sem, 2)
            act.wait_ge(s_x, 16)
            act.wait_ge(s_cst, 48)
            with act.Fori(0, DEPTH) as L:
                acs.n = 0
                hi_unit(L, 0, 0)
                hi_unit(L, 1, 1)
                act.wait_ge(parl.sem, L * 16 + 16)
                act.wait_ge(res.sem, res.at(L, 0))
                for r in range(4):
                    last = nc.scalar.activation(glr_hi[:, :, r], glr_w, ACT.Copy)
                last.then_inc(glrw.sem, 1)
                for kt in range(KT):
                    act.wait_ge(res.sem, L * 2 * KT + 1)
                    square(L, kt, x[:, kt])
                    if kt == 3:
                        sine_of(L, 0, hid1, FFN_HY)
                sine_of(L, 1, hid_a, P)
                root(L, 0, rstd[:, :])
                for kt in range(KT):
                    round_tile(L, kt, kt, nrm[:, kt % 2])
                for slot in range(U_OUT):
                    before(L, slot)
                    hi_unit(L, slot + RING, slot % RING)
                    evacuate(L, slot)
                    after(L, slot)
                before(L, U_OUT)
                turn_copy(L, 0)
                before(L, U_OUT + 2)
                turn_copy(L, 1)
                for h in range(HEADS):
                    act.wait_ge(oc.sem, oc.at(L, h + 1))
                    square(L, 8 + h, o_t[:, h])
                for h in range(HEADS):
                    root(L, 1 + h, o_rstd[:, h])
                act.wait_ge(evac.sem, evac.at(L, 12))
                nc.scalar.activation(r_t[:, :], r_t[:, :], ACT.Silu).then_inc(silu_r.sem, 1)
                for c in range(CT):
                    act.wait_ge(gated.sem, gated.at(L, 4 + c + 1))
                    square(L, 12 + c, u[:, 8 + c])
                act.wait_ge(unit.sem, unit.at(L, U_OUT))
                for h in range(HEADS):
                    round_tile(L, 8 + h, h, o_t[:, h])
                root(L, 5, rstd[:, :])
                for c in range(CT):
                    round_tile(L, 12 + c, 4 + c, u[:, 8 + c])
                for m in range(KT):
                    hi_unit(L, U_OUT + m + RING, m % RING)
                    act.wait_ge(res.sem, res.at(L, m + 1))
                    square(L, 16 + m, x[:, m])
                root(L, 6, rstd[:, :])
                for kt in range(KT):
                    round_tile(L, 16 + kt, kt, nrm[:, kt % 2])
                with act.Fori(0, FT // 2) as i:
                    for j in range(4):
                        act.wait_ge(unit.sem, L * UNITS + i * 4 + (U_FFN + j + 1 + RING))
                        hi_unit(L, U_FFN + j + RING, j % RING, i, 4)
                        n = j // 2
                        if j % 2 == 0:
                            act.wait_ge(hidn.sem, L * FT + i * 2 + (n + 1))
                            nc.scalar.activation(sg[:, n], ps[:, j, :], ACT.Silu).then_inc(gate.sem, 1)
                        else:
                            act.wait_ge(hidn.sem, L * FT + i * 2 + (n + 1 + 2))
                            nc.scalar.activation(hid_hi[:, i * 2 + n, :], nrm[:, n], ACT.Copy)\
                                .then_inc(hhi.sem, 1)
                with act.Fori(0, (FT - RING) // RING) as i:
                    for j in range(RING):
                        hi_unit(L, U_DOWN + j + RING, j, i, RING)
            for kt in range(KT):
                act.wait_ge(res.sem, res.at(DEPTH, 0))
                square(DEPTH, kt, x[:, kt])
            root(DEPTH, 0, rstd[:, :])
            assert acs.n == acs.per_layer, acs.n

        @block.gpsimd
        def _(pool):
            def lo_unit(L, n, j, i=None, per=0):
                at = n if i is None else i * per + n
                pool.wait_ge(hi.sem, L * UNITS + at + 1)
                nc.gpsimd.tensor_tensor(w_lo[:, j], w_raw[:, j], w_hi[:, j].bitcast(F32),
                                        ALU.subtract).then_inc(lo.sem, 1)

            def rest_tile(L, n, kt, src):
                pool.wait_ge(ahi.sem, ahi.at(L, n + 1))
                nc.gpsimd.tensor_tensor(h_lo[:, kt], src, h_hi[:, kt].bitcast(F32),
                                        ALU.subtract).then_inc(alo.sem, 1)

            nc.gpsimd.memset(ones[:, :], 1.0).then_inc(s_ones, 1)
            pool.sem_inc(lo.sem, RING)
            pool.sem_inc(alo.sem, 2)
            pool.sem_inc(hlo.sem, 2)
            with pool.Fori(0, DEPTH) as L:
                lo_unit(L, 0, 0)
                lo_unit(L, 1, 1)
                pool.wait_ge(glrw.sem, L * 2 + 1)
                for r in range(4):
                    last = nc.gpsimd.tensor_tensor(glr_lo[:, :, r], glr_w, glr_hi[:, :, r].bitcast(F32),
                                                   ALU.subtract)
                last.then_inc(glrw.sem, 1)
                for kt in range(KT):
                    rest_tile(L, kt, kt, nrm[:, kt % 2])
                for slot in range(U_OUT):
                    lo_unit(L, slot + RING, slot % RING)

                def spectra(o):
                    for s in range(NSEQ):
                        for i in range(2):
                            n = 4 * o + 2 * s + i
                            pool.wait_ge(prd.sem, prd.at(L, n + 1))
                            re, im = spec[s][:, 2 * i], spec[s][:, 2 * i + 1]
                            nc.gpsimd.tensor_tensor(re, re, prod[:, 2 * i], ALU.subtract)
                            nc.gpsimd.tensor_tensor(im, im, prod[:, 2 * i + 1], ALU.add).then_inc(yfd.sem, 1)

                spectra(0)
                spectra(1)
                for h in range(HEADS):
                    rest_tile(L, 8 + h, h, o_t[:, h])
                for c in range(CT):
                    rest_tile(L, 12 + c, 4 + c, u[:, 8 + c])
                for m in range(KT):
                    lo_unit(L, U_OUT + m + RING, m % RING)
                for kt in range(KT):
                    rest_tile(L, 16 + kt, kt, nrm[:, kt % 2])
                with pool.Fori(0, FT // 2) as i:
                    for j in range(4):
                        lo_unit(L, U_FFN + j + RING, j % RING, i, 4)
                        n = j // 2
                        if j % 2:
                            pool.wait_ge(hhi.sem, L * FT + i * 2 + (n + 1))
                            nc.gpsimd.tensor_tensor(hid_lo[:, i * 2 + n, :], nrm[:, n],
                                                    hid_hi[:, i * 2 + n, :].bitcast(F32),
                                                    ALU.subtract).then_inc(hlo.sem, 1)
                with pool.Fori(0, (FT - RING) // RING) as i:
                    for j in range(RING):
                        lo_unit(L, U_DOWN + j + RING, j, i, RING)

        @block.vector
        def _(v):
            def mean_square(L, n, bank, width, t):
                a = dve.next(L)
                nc.vector.tensor_scalar(t, ps[:, bank, :], 1.0 / width, EPS, ALU.mult, ALU.add)\
                    .then_inc(dve.sem, 1)
                v.wait_ge(dve.sem, a)
                nc.vector.reciprocal(t, t).then_inc(inv_ms.sem, 1)

            def normalise(L, first_n, count, src, gain):
                for n in range(count):
                    v.wait_ge(alo.sem, alo.at(L, first_n + n - 1))
                    nc.vector.scalar_tensor_tensor(out=nrm[:, n % 2], in0=src[:, n], scalar=gain(n),
                                                   in1=rstd[:, :], op0=ALU.mult, op1=ALU.mult)\
                        .then_inc(normed.sem, 1)

            def reduce_turn(L, n, rows, bank, b, f):
                t = arg[0:rows, :]
                k = turn[0:rows, :]
                v.wait_ge(net.sem, net.at(L, n + 1))
                if n:
                    v.wait_ge(sine.sem, sine.at(L, n))
                a = dve.next(L)
                nc.vector.tensor_scalar(t, ps[0:rows, bank, 0:SEQ], par[0:rows, b:b + 1], par[0:rows, f:f + 1],
                                        ALU.add, ALU.mult).then_inc(dve.sem, 1)
                v.wait_ge(dve.sem, a)
                magic = 1.5 * 2.0 ** 23
                a = dve.next(L)
                nc.vector.tensor_scalar(k, t, 1.0 / (2 * math.pi), magic, ALU.mult, ALU.add).then_inc(dve.sem, 1)
                v.wait_ge(dve.sem, a)
                a = dve.next(L)
                nc.vector.tensor_scalar(k, k, -magic, None, ALU.add).then_inc(dve.sem, 1)
                v.wait_ge(dve.sem, a)
                for c in TURN_PARTS:
                    a = dve.next(L)
                    nc.vector.scalar_tensor_tensor(out=t, in0=k, scalar=-c, in1=t, op0=ALU.mult,
                                                   op1=ALU.add).then_inc(dve.sem, 1)
                    v.wait_ge(dve.sem, a)
                nc.vector.tensor_scalar(t, t, PI_BELOW, -PI_BELOW, ALU.min, ALU.max).then_inc(turned.sem, 1)

            def window(L, o):
                for n in range(4):
                    t, k = divmod(n, 2)
                    if n == 0 and o:
                        v.wait_ge(kfp.sem, kfp.at(L, 5))
                    v.wait_ge(abp.sem, abp.at(L, 4 * o + n + 1))
                    nc.vector.tensor_tensor(ab[:, t, k], ps[:, 2 + n, :], win[:, t], ALU.mult)\
                        .then_inc(abw.sem, 1)

            def gate_sums(L, h):
                v.wait_ge(zabs.sem, zabs.at(L, h + 1))
                nc.vector.tensor_scalar(xx[:, h], ps[:, 2 + h, :], par[:, C_BG + h:C_BG + h + 1], 0.0,
                                        ALU.add, ALU.min).then_inc(zmin.sem, 1)
                v.wait_ge(zln.sem, zln.at(L, h + 1))
                v.wait_ge(zmin.sem, zmin.at(L, h + 1))
                for s in range(NSEQ):
                    cols = slice(SEQ * s, SEQ * s + SEQ)
                    last = nc.vector.tensor_tensor_scan(pre[:, h, s, 1:SEQ + 1], xx[:, h, cols], dd[:, h, cols],
                                                        0.0, ALU.add, ALU.subtract)
                last.then_inc(scan.sem, 1)
                v.wait_ge(scan.sem, scan.at(L, h + 1))
                b = bt[:, h].rearrange("p (s t) -> p s t", s=NSEQ)
                nc.vector.tensor_copy(b[0:DK], pre[0:DK, h, :, 1:SEQ + 1])
                nc.vector.tensor_copy(b[DK:P], pre[DK:P, h, :, 0:SEQ]).then_inc(btd.sem, 1)

            def split(t, s, seqs=None):
                return t.rearrange("p (q n e s) -> p q n e s", q=NSEQ, e=2, s=s)

            def exponents(L, slot):
                hp = head_pair(slot + 1)
                if not hp:
                    return
                h, p = hp
                for l in (2 * p, 2 * p + 1):
                    s, n = LEVELS[l], lvl(h, l)
                    if l == 0:
                        v.wait_ge(btd.sem, btd.at(L, h + 1))
                    if n >= 4:
                        v.wait_ge(xld.sem, xld.at(L, n - 3))
                    else:
                        v.wait_ge(scan.sem, scan.at(L, HEADS))
                    d, b = split(dd[:, n % 4], s), split(bt[:, h], s)
                    for q in range(NSEQ):
                        m = pre[:, h, q, s:SEQ:2 * s].unsqueeze(2).to_broadcast([P, SEQ // (2 * s), s])
                        nc.vector.tensor_tensor(d[:, q, :, 0], m, b[:, q, :, 0], ALU.subtract)
                        last = nc.vector.tensor_tensor(d[:, q, :, 1], b[:, q, :, 1], m, ALU.subtract)
                    last.then_inc(expo.sem, 1)

            def scaled(L, slot):
                hp = head_pair(slot)
                if not hp:
                    return
                h, p = hp
                for l in (2 * p, 2 * p + 1):
                    s, n = LEVELS[l], lvl(h, l)
                    v.wait_ge(fact.sem, fact.at(L, n + 1))
                    if h == 0 and l == 0:
                        v.wait_ge(evac.sem, evac.at(L, 4))
                    if n >= 4:
                        v.wait_ge(pair.sem, pair.at(L, (n - 4) // 2 + 1))
                    f, o = split(dd[:, n % 4], s), split(xx[:, n % 4], s)
                    for e, g in ((0, g1), (1, g2)):
                        gg = split(g[:, h], s)
                        last = nc.vector.tensor_tensor(
                            o[:, :, :, e].rearrange("p q n s -> p (q n) s"),
                            gg[:, :, :, e].rearrange("p q n s -> p (q n) s"),
                            f[:, :, :, e].rearrange("p q n s -> p (q n) s"), ALU.mult)
                    last.then_inc(xld.sem, 1)

            def put_levels(L, slot):
                hp = head_pair(slot - 2)
                if not hp or hp[1] == 0:
                    return
                h, p = hp
                v.wait_ge(pair.sem, pair.at(L, 4 * h + p + 1))
                if p == 1:
                    v.wait_ge(big.sem, big.at(L, h + 1))
                done = 10 * h + (0, 0, 2, 6)[p]
                for l in ((3,) if p == 1 else (2 * p, 2 * p + 1)):
                    for way in range(2):
                        bank = (4 if l % 2 else 2) + way
                        if done:
                            v.wait_ge(put.sem, put.at(L, done))
                        nc.vector.tensor_copy(carrier[:, 0:1], mask[:, 0, 0, 0:1])
                        nc.vector.copy_predicated(
                            amat[:, 0].rearrange("p s j i -> p (s j) i"),
                            mask[:, l - 3, way].unsqueeze(1).to_broadcast([P, 4, P]),
                            ps[:, bank, :].rearrange("p (n c) -> p n c", n=4)).then_inc(put.sem, 1)
                        done += 1

            def short_conv(L, slot):
                t = slot
                if U_HV <= t < U_R:
                    c = t - U_HV
                    b = ps[:, t % 2, :].rearrange("p (s t) -> p s t", s=NSEQ)
                    v.wait_ge(mid.sem, mid.at(L, c + 1))
                    a = dve.next(L)
                    nc.vector.scalar_tensor_tensor(out=u_seq[:, c, :, 1:SEQ], in0=b[:, :, 0:SEQ - 1],
                                                   scalar=par[:, C_CW + c:C_CW + c + 1], in1=u_seq[:, c, :, 1:SEQ],
                                                   op0=ALU.mult, op1=ALU.add).then_inc(dve.sem, 1)
                    v.wait_ge(dve.sem, a)
                    nc.vector.scalar_tensor_tensor(out=u_seq[:, c, :, 0:SEQ - 1], in0=b[:, :, 1:SEQ],
                                                   scalar=par[:, C_CW + 24 + c:C_CW + 25 + c],
                                                   in1=u_seq[:, c, :, 0:SEQ - 1],
                                                   op0=ALU.mult, op1=ALU.add).then_inc(conv.sem, 1)

            def products(L, o):
                if o:
                    v.wait_ge(invp.sem, invp.at(L, 4))
                for s in range(NSEQ):
                    for i in range(2):
                        n = 4 * o + 2 * s + i
                        banks = (0, 1, 6, 7)
                        ur, ui = ps[:, banks[2 * i], :], ps[:, banks[2 * i + 1], :]
                        kr, ki = kf[:, o, i], kf[:, o, 3 + i]
                        kr2 = kf[:, o, 2] if i == 0 else kr
                        v.wait_ge(ufp.sem, ufp.at(L, 8 * o + 4 * s + 2 * i + 2))
                        if n >= 2:
                            v.wait_ge(yfd.sem, yfd.at(L, n - 1))
                        nc.vector.tensor_tensor(spec[s][:, 2 * i], ur, kr, ALU.mult)
                        nc.vector.tensor_tensor(prod[:, 2 * i], ui, ki, ALU.mult)
                        nc.vector.tensor_tensor(prod[:, 2 * i + 1], ur, ki, ALU.mult)
                        nc.vector.tensor_tensor(spec[s][:, 2 * i + 1], ui, kr2, ALU.mult).then_inc(prd.sem, 1)

            def gating(L, o):
                for c in range(CT):
                    v.wait_ge(invp.sem, invp.at(L, 4 * o + c + 1))
                    z = u[:, 4 * (o + 1) + c]
                    nc.vector.tensor_tensor(z, ps[:, 2 + c, :], z, ALU.mult).then_inc(gated.sem, 1)

            def residual(L, base_n, m, bank):
                nc.vector.tensor_tensor(x[:, m], x[:, m], ps[:, bank, :], ALU.add).then_inc(res.sem, 1)

            a = nc.vector.memset(pre_t[:, :], 0.0)
            a.then_inc(s_pre0, 1)
            v.sem_inc(res.sem, 1)
            v.sem_inc(normed.sem, 1)
            v.sem_inc(hidn.sem, 2)
            v.wait_ge(s_x, 16)
            v.wait_ge(s_cst, 48)
            nc.vector.tensor_copy(mask.rearrange("p l d c -> p (l d c)"), mask_f).then_inc(s_pre0, 1)
            v.wait_ge(s_pre0, 2)
            with v.Fori(0, DEPTH) as L:
                dve.n = 0
                v.wait_ge(parl.sem, L * 16 + 16)
                reduce_turn(L, 0, FFN_HY, 5, C_B1, C_F1)
                reduce_turn(L, 1, P, 4, C_B2, C_F2)
                v.wait_ge(sine.sem, sine.at(L, 2))
                nc.vector.tensor_copy(hid_b[0:FFN_HY, :], hid_a[0:FFN_HY, :])
                a = dve.next(L)
                nc.vector.tensor_scalar(hid_b[FFN_HY:P, :], hid_a[FFN_HY:P, :], -1.0, None, ALU.mult)\
                    .then_inc(dve.sem, 1)
                v.wait_ge(dve.sem, a)
                nc.vector.memset(hid_a[FFN_HY:P, 0:1], 0.0).then_inc(hidab.sem, 1)
                v.wait_ge(stat.sem, stat.at(L, KT))
                mean_square(L, 0, 7, D_MODEL, rstd[:, :])
                v.wait_ge(rms.sem, rms.at(L, 1))
                normalise(L, 0, KT, x, lambda n: par[:, C_NMIX + n:C_NMIX + n + 1])
                window(L, 0)
                for slot in range(U_OUT):
                    if slot == 1:
                        window(L, 1)
                    if slot == 2:
                        a = dve.next(L)
                        nc.vector.memset(pre[:, :, :, 0:1], 0.0).then_inc(dve.sem, 1)
                        v.wait_ge(dve.sem, a)
                        for h in range(HEADS):
                            gate_sums(L, h)
                    put_levels(L, slot)
                    exponents(L, slot)
                    scaled(L, slot)
                    short_conv(L, slot)
                put_levels(L, U_OUT)
                put_levels(L, U_OUT + 1)
                products(L, 0)
                gating(L, 0)
                for h in range(HEADS):
                    v.wait_ge(stat.sem, stat.at(L, 8 + h + 1))
                    if h == 0:
                        v.wait_ge(op_.sem, op_.at(L, HEADS))
                    nc.vector.tensor_scalar(o_rstd[:, h], ps[:, 2 + h, :], 1.0 / DV, EPS, ALU.mult, ALU.add)\
                        .then_inc(o_ms.sem, 1)
                products(L, 1)
                for h in range(HEADS):
                    v.wait_ge(o_ms.sem, o_ms.at(L, h + 1))
                    nc.vector.reciprocal(o_rstd[:, h], o_rstd[:, h]).then_inc(inv_ms.sem, 1)
                gating(L, 1)
                for h in range(HEADS):
                    v.wait_ge(rms.sem, rms.at(L, 2 + h))
                    a = dve.next(L)
                    nc.vector.scalar_tensor_tensor(out=o_t[:, h], in0=o_t[:, h], scalar=par[:, C_GN:C_GN + 1],
                                                   in1=o_rstd[:, h], op0=ALU.mult, op1=ALU.mult)\
                        .then_inc(dve.sem, 1)
                    v.wait_ge(dve.sem, a)
                    if h == 0:
                        v.wait_ge(silu_r.sem, silu_r.at(L, 1))
                    nc.vector.tensor_tensor(o_t[:, h], o_t[:, h], r_t[:, h], ALU.mult).then_inc(normed.sem, 1)
                v.wait_ge(stat.sem, stat.at(L, 16))
                mean_square(L, 5, 6, HY, rstd[:, :])
                v.wait_ge(rms.sem, rms.at(L, 6))
                for c in range(CT):
                    nc.vector.scalar_tensor_tensor(out=u[:, 8 + c], in0=u[:, 8 + c],
                                                   scalar=par[:, C_HN + c:C_HN + c + 1], in1=rstd[:, :],
                                                   op0=ALU.mult, op1=ALU.mult).then_inc(normed.sem, 1)
                for m in range(KT):
                    v.wait_ge(unit.sem, unit.at(L, U_OUT + m + 1))
                    residual(L, 0, m, m % 2)
                v.wait_ge(stat.sem, stat.at(L, 24))
                mean_square(L, 6, 7, D_MODEL, rstd[:, :])
                v.wait_ge(rms.sem, rms.at(L, 7))
                normalise(L, 16, KT, x, lambda n: par[:, C_NFFN + n:C_NFFN + n + 1])
                with v.Fori(0, FT // 2) as i:
                    for n in range(2):
                        v.wait_ge(unit.sem, L * UNITS + i * 4 + (U_FFN + 2 * n + 2 + RING))
                        v.wait_ge(gate.sem, L * FT + i * 2 + (n + 1 + 2))
                        v.wait_ge(hlo.sem, L * FT + i * 2 + (n + 1))
                        nc.vector.tensor_tensor(nrm[:, n], ps[:, 2 * n + 1, :], sg[:, n], ALU.mult)\
                            .then_inc(hidn.sem, 1)
                for m in range(KT):
                    v.wait_ge(down.sem, down.at(L, m + 1))
                    residual(L, KT, m, m)
            assert dve.n == dve.per_layer, dve.n
            dve.n = 0
            v.wait_ge(stat.sem, stat.at(DEPTH, KT))
            mean_square(DEPTH, 0, 7, D_MODEL, rstd[:, :])
            v.wait_ge(rms.sem, rms.at(DEPTH, 1))
            for kt in range(KT):
                nc.vector.scalar_tensor_tensor(out=x[:, kt], in0=x[:, kt], scalar=fin[:, kt:kt + 1],
                                               in1=rstd[:, :], op0=ALU.mult, op1=ALU.mult)\
                    .then_inc(normed.sem, 1)

        @block.tensor
        def _(pe):
            def passes(bank, slot, b, act_hi, act_lo, start, stop):
                out = ps[:, bank, :]
                nc.tensor.matmul(out, w_hi[:, slot, b], act_hi, start=start, stop=False)
                nc.tensor.matmul(out, w_hi[:, slot, b], act_lo, start=False, stop=False)
                return nc.tensor.matmul(out, w_lo[:, slot, b], act_hi, start=False, stop=stop)

            def sum_square(L, n, bank, start, stop):
                pe.wait_ge(sqd.sem, sqd.at(L, n + 1))
                nc.tensor.matmul(ps[:, bank, :], ones[:, :], sq[:, n % 2], start=start, stop=stop)\
                    .then_inc(stat.sem, 1)

            def filters(L, o):
                w3 = par[:, C_W3 + o * HY:C_W3 + (o + 1) * HY]
                skip = par[:, C_MISC + o * HY:C_MISC + (o + 1) * HY]
                for n in range(4):
                    t, k = divmod(n, 2)
                    if o:
                        pe.wait_ge(kfc.sem, kfc.at(L, 5))
                    elif n == 0:
                        pe.wait_ge(hidab.sem, hidab.at(L, 1))
                    h = (hid_a, hid_b)[k][:, t * P:(t + 1) * P]
                    last = nc.tensor.matmul(ps[:, 2 + n, :], h, w3, start=True, stop=n != 0)
                    if n == 0:
                        last = nc.tensor.matmul(ps[:, 2, :], skip_sel, skip, start=False, stop=True)
                    last.then_inc(abp.sem, 1)

            def filter_spectra(L, o):
                for f, (c, k) in enumerate(((DFT_C0, 0), (DFT_C1, 0), (DFT_C0N, 0), (DFT_S0, 1), (DFT_S1, 1))):
                    if f == 0:
                        pe.wait_ge(abw.sem, abw.at(L, 4 * o + 4))
                    if f == 4:
                        pe.wait_ge(glrt.sem, glrt.at(L, 1))
                    for t in range(2):
                        last = nc.tensor.matmul(ps[:, 2 + f, :], dft[:, c, t], ab[:, t, k], start=t == 0, stop=t == 1)
                    last.then_inc(kfp.sem, 1)

            def level_pair(L, h, p):
                n = lvl(h, 2 * p + 1)
                pe.wait_ge(xld.sem, xld.at(L, n + 1))
                if p == 0:
                    if h == 0:
                        pe.wait_ge(scan.sem, scan.at(L, HEADS))
                    if h == 1:
                        pe.wait_ge(vtc.sem, vtc.at(L, HEADS))
                    if h >= 1:
                        pe.wait_ge(oc.sem, oc.at(L, h))
                    for s in range(NSEQ):
                        for j in range(2):
                            t = slice(SEQ * s + P * j, SEQ * s + P * j + P)
                            nc.tensor.matmul(ps[:, 6 + s, P * j:P * j + P],
                                             g1[:, h, t], g2[:, h, t], start=True, stop=True)
                else:
                    if p >= 2:
                        pe.wait_ge(put.sem, put.at(L, 10 * h + (0, 0, 2, 6)[p]))
                        pe.wait_ge(big.sem, big.at(L, h + 1))
                for l in (2 * p + 1, 2 * p):
                    s, xl = LEVELS[l], xx[:, lvl(h, l) % 4]
                    for way in range(2):
                        rows = slice(DK * way, DK * way + DK)
                        if s >= 32:
                            for q in range(NSEQ):
                                for n in range(SEQ // (2 * s)):
                                    low, up = 2 * s * n, 2 * s * n + s
                                    j, i = (low, up) if way == 0 else (up, low)
                                    col = P * (j // P) + (i % P if s < P else SEQ)
                                    out = ps[j % P:j % P + s, (6 if way == 0 else 2) + q, col:col + s]
                                    last = nc.tensor.matmul(out, xl[rows, SEQ * q + j:SEQ * q + j + s],
                                                            xl[rows, SEQ * q + i:SEQ * q + i + s],
                                                            start=True, stop=True)
                        else:
                            bank = (4 if l % 2 else 2) + way
                            for n in range(4):
                                t = xl[rows, P * n:P * n + P]
                                last = nc.tensor.matmul(ps[:, bank, P * n:P * n + P], t, t, start=True, stop=True)
                last.then_inc(pair.sem, 1)

            def turn_v(L, h):
                if h == 0:
                    pe.wait_ge(evac.sem, evac.at(L, 8))
                    pe.wait_ge(big.sem, big.at(L, 1))
                if h >= 2:
                    pe.wait_ge(vtc.sem, vtc.at(L, h - 1))
                for t in range(TT):
                    last = nc.tensor.transpose(ps[:, 6 + h % 2, P * t:P * t + P],
                                               u[:, 8 + h, P * t:P * t + P], ident)
                last.then_inc(vtp.sem, 1)

            def attend(L, h):
                pe.wait_ge(put.sem, put.at(L, 10 * h + 10))
                pe.wait_ge(vtc.sem, vtc.at(L, HEADS))
                for s in range(NSEQ):
                    for i in range(2):
                        for j in range(2):
                            c = SEQ * s + P * i
                            last = nc.tensor.matmul(ps[:, 2, c:c + P], v_tok[:, h, 2 * s + j],
                                                    amat[:, int(i != j), s, j], start=j == 0, stop=j == 1)
                last.then_inc(op_.sem, 1)

            def side(L, slot):
                if slot == 0:
                    filter_spectra(L, 0)
                if slot == 1:
                    filters(L, 1)
                    filter_spectra(L, 1)
                if slot == 2:
                    for h in range(HEADS):
                        if h == 0:
                            pe.wait_ge(kfc.sem, kfc.at(L, 10))
                        nc.tensor.matmul(ps[:, 2 + h, :], par[0:2 * RANK, C_MISC + P * h:C_MISC + P * h + P],
                                         glr_t[0:2 * RANK, :], start=True, stop=True).then_inc(zp.sem, 1)
                if slot == 8:
                    turn_v(L, 0)
                    turn_v(L, 1)
                if slot == 9:
                    turn_v(L, 2)
                    turn_v(L, 3)
                hp = head_pair(slot - 1)
                if hp:
                    level_pair(L, *hp)
                for h in range(HEADS):
                    if slot == first(h) + 5:
                        attend(L, h)

            def turn_tokens(L, o):
                for t in range(TT):
                    for c in range(CT):
                        if t == 0:
                            if o == 0 and c == 0:
                                pe.wait_ge(conv.sem, conv.at(L, 4))
                                pe.wait_ge(evac.sem, evac.at(L, 12))
                                pe.wait_ge(big.sem, big.at(L, HEADS))
                            if o == 1:
                                pe.wait_ge(gated.sem, gated.at(L, c + 1))
                        last = nc.tensor.transpose(ps[:, (0, 1, 6, 7)[t], P * c:P * c + P],
                                                   u[:, 4 * o + c, P * t:P * t + P], ident)
                    last.then_inc(utp.sem, 1)

            def spectrum(L, o, s):
                pe.wait_ge(utc.sem, utc.at(L, 4 * o + 4))
                for f, c in enumerate((DFT_C0, DFT_S0N, DFT_C1, DFT_S1)):
                    if s and f % 2 == 0:
                        pe.wait_ge(prd.sem, prd.at(L, 4 * o + f // 2 + 1))
                    for t in range(2):
                        last = nc.tensor.matmul(ps[:, (0, 1, 6, 7)[f], :], dft[:, c, t], u_tok[:, 2 * s + t],
                                                start=t == 0, stop=t == 1)
                    last.then_inc(ufp.sem, 1)

            def back(L, o, s):
                pe.wait_ge(yfd.sem, yfd.at(L, 4 * o + 2 * s + 2))
                for c in range(CT):
                    for f in range(4):
                        last = nc.tensor.matmul(ps[:, 2 + c, SEQ * s:SEQ * s + SEQ],
                                                spec[s][:, f, P * c:P * c + P], inv[:, f],
                                                start=f == 0, stop=f == 3)
                    if s:
                        last.then_inc(invp.sem, 1)

            pe.sem_inc(unit.sem, RING)
            pe.sem_inc(stat.sem, 2)
            pe.wait_ge(s_cst, 48)
            pe.wait_ge(s_ones, 1)
            with pe.Fori(0, DEPTH) as L:
                pe.wait_ge(parl.sem, L * 16 + 16)
                pe.wait_ge(res.sem, res.at(L, 0))
                nc.tensor.matmul(ps[0:FFN_HY, 5, 0:SEQ], par[0:EMB, C_W1:C_W1 + FFN_HY], feat, start=True,
                                 stop=True).then_inc(net.sem, 1)
                for kt in range(KT):
                    sum_square(L, kt, 7, kt == 0, kt == KT - 1)
                    if kt == 4:
                        pe.wait_ge(sine.sem, sine.at(L, 1))
                        nc.tensor.matmul(ps[:, 4, 0:SEQ], par[0:FFN_HY, C_W2:C_W2 + P], hid1[0:FFN_HY, :],
                                         start=True, stop=True).then_inc(net.sem, 1)
                filters(L, 0)
                pe.wait_ge(glrw.sem, L * 2 + 2)
                for kt in range(KT):
                    pe.wait_ge(alo.sem, alo.at(L, kt + 1))
                    wh = glr_hi[:, kt].rearrange("p r c -> p (r c)")
                    wl = glr_lo[:, kt].rearrange("p r c -> p (r c)")
                    nc.tensor.matmul(ps[:, 6, :], wh, h_hi[:, kt], start=kt == 0, stop=False)
                    nc.tensor.matmul(ps[:, 6, :], wh, h_lo[:, kt], start=False, stop=False)
                    last = nc.tensor.matmul(ps[:, 6, :], wl, h_hi[:, kt], start=False, stop=kt == KT - 1)
                last.then_inc(glrp.sem, 1)
                for t in range(U_OUT):
                    pe.wait_ge(lo.sem, lo.at(L, t + 1))
                    if 2 <= t < U_HV + 2:
                        pe.wait_ge(evac.sem, evac.at(L, t - 1))
                    elif U_HV + 2 <= t < U_R + 2:
                        pe.wait_ge(conv.sem, conv.at(L, t - 1 - U_HV))
                    elif t >= U_R + 2:
                        pe.wait_ge(evac.sem, evac.at(L, t - 1 - 12))
                    for kt in range(KT):
                        last = passes(t % 2, t % 2, kt, h_hi[:, kt], h_lo[:, kt], kt == 0, kt == KT - 1)
                    last.then_inc(unit.sem, 1)
                    side(L, t)
                side(L, U_OUT)
                turn_tokens(L, 0)
                side(L, U_OUT + 1)
                spectrum(L, 0, 0)
                spectrum(L, 0, 1)
                pe.wait_ge(oc.sem, oc.at(L, HEADS))
                back(L, 0, 0)
                back(L, 0, 1)
                turn_tokens(L, 1)
                for h in range(HEADS):
                    sum_square(L, 8 + h, 2 + h, True, True)
                spectrum(L, 1, 0)
                spectrum(L, 1, 1)
                pe.wait_ge(o_ms.sem, o_ms.at(L, HEADS))
                back(L, 1, 0)
                back(L, 1, 1)
                for c in range(CT):
                    sum_square(L, 12 + c, 6, c == 0, c == CT - 1)
                pe.wait_ge(prd.sem, prd.at(L, 8))
                for m in range(2):
                    pe.wait_ge(lo.sem, lo.at(L, U_OUT + m + 1))
                    for kt in range(HEADS):
                        pe.wait_ge(alo.sem, alo.at(L, 8 + kt + 1))
                        passes(m, m, kt, h_hi[:, kt], h_lo[:, kt], kt == 0, False)
                for m in range(KT):
                    if m >= 2:
                        pe.wait_ge(lo.sem, lo.at(L, U_OUT + m + 1))
                        pe.wait_ge(res.sem, res.at(L, m - 1))
                    for kt in range(HEADS if m < 2 else 0, KT):
                        if m == 0:
                            pe.wait_ge(alo.sem, alo.at(L, 8 + kt + 1))
                        last = passes(m % 2, m % 2, kt, h_hi[:, kt], h_lo[:, kt], kt == 0, kt == KT - 1)
                    last.then_inc(unit.sem, 1)
                    if m:
                        sum_square(L, 16 + m - 1, 7, m == 1, False)
                sum_square(L, 16 + KT - 1, 7, False, True)
                with pe.Fori(0, FT // 2) as i:
                    for j in range(4):
                        pe.wait_ge(lo.sem, L * UNITS + i * 4 + (U_FFN + j + 1 + RING))
                        if j % 2 == 0:
                            pe.wait_ge(gate.sem, L * FT + i * 2 + (j // 2 + 1))
                        else:
                            pe.wait_ge(hidn.sem, L * FT + i * 2 + (j // 2 + 1))
                        for kt in range(KT):
                            if j == 0:
                                pe.wait_ge(alo.sem, alo.at(L, 16 + kt + 1))
                            last = passes(j, j % 2, kt, h_hi[:, kt], h_lo[:, kt], kt == 0, kt == KT - 1)
                        last.then_inc(unit.sem, 1)

                def down_unit(f, slot, need, start, stop):
                    pe.wait_ge(lo.sem, need)
                    for m in range(KT):
                        last = passes(m, slot, m, hid_hi[:, f, :], hid_lo[:, f, :], start, stop)
                        if stop:
                            last.then_inc(down.sem, 1)
                    return last

                pe.wait_ge(hlo.sem, hlo.at(L, FT))
                for f in range(2):
                    down_unit(f, f, lo.at(L, U_DOWN + f + 1), f == 0, False).then_inc(unit.sem, 1)
                with pe.Fori(0, (FT - 4) // 2) as i:
                    for j in range(2):
                        down_unit(i * 2 + (2 + j), j, L * UNITS + i * 2 + (U_DOWN + 2 + j + 1 + RING),
                                  False, False).then_inc(unit.sem, 1)
                for f in range(FT - 2, FT):
                    last = down_unit(f, f % 2, lo.at(L, U_DOWN + f + 1), False, f == FT - 1)
                    if f < FT - 1:
                        last.then_inc(unit.sem, 1)
                nc.tensor.drain().then_inc(unit.sem, 1)
            pe.wait_ge(res.sem, res.at(DEPTH, 0))
            for kt in range(KT):
                sum_square(DEPTH, kt, 7, kt == 0, kt == KT - 1)


TURN_PARTS = (6.28125, 0.0019350051879882812, 3.019916050561733e-07)
PI_BELOW = 3.1415925


def constants():
    t = np.arange(SEQ)
    f = np.arange(P)
    n = 2 * SEQ

    def angle(rows, cols):
        return 2 * np.pi * ((rows[:, None] * cols[None, :]) % n) / n

    c0, s0 = np.cos(angle(t, f)), -np.sin(angle(t, f))
    c1, s1 = np.cos(angle(t, f + P)), -np.sin(angle(t, f + P))
    alternate = np.where(t % 2, -1.0, 1.0)
    c0n, s0n = c0.copy(), s0.copy()
    c0n[:, 0] = alternate
    s0n[:, 0] = alternate
    s0[:, 0] = 0.0
    dft = np.stack([c0, c1, c0n, s0, s0n, s1])
    dft = dft.reshape(6, 2, P, P).transpose(2, 0, 1, 3).reshape(P, -1)
    back = np.stack([c0.T, s0.T, c1.T, s1.T]) * 2.0 / n
    back[0, 0] = 1.0 / n
    back[1, 0] = alternate / n
    back = back.transpose(1, 0, 2).reshape(P, -1)
    pos = np.linspace(0.0, 1.0, SEQ, dtype=np.float32)
    w = (np.float32(2.0 * math.pi / SEQ) * np.arange(SEQ, dtype=np.float32))[:, None]
    bands = np.linspace(1e-4, 7.0, 8, dtype=np.float32)
    feats = np.concatenate([pos[:, None], np.cos(bands * w), -np.sin(bands * w)], axis=-1)
    slow, fast = math.log(1e-2) / 1.5, math.log(1e-2) / 0.3
    deltas = np.abs(np.linspace(slow, fast, HY, dtype=np.float32))
    win = np.exp(-pos[:, None] * deltas).reshape(2, P, HY).transpose(1, 0, 2).reshape(P, -1)
    mid = np.zeros((P, SEQ))
    mid[:EMB] = feats.T
    cst = np.concatenate([np.eye(P, P + P // 2), mid, dft, back, win], axis=1).astype(np.float32)
    masks = np.zeros((P, len(MASKED), 2, P), np.float32)
    j, i = np.meshgrid(np.arange(P), np.arange(P), indexing="ij")
    for l, s in enumerate(MASKED):
        same = j // (2 * s) == i // (2 * s)
        masks[:, l, 0] = same & (j // s % 2 == 0) & (i // s % 2 == 1)
        masks[:, l, 1] = same & (j // s % 2 == 1) & (i // s % 2 == 0)
    return cst, masks.reshape(P, -1)


def columns(v):
    return v.reshape(-1, P).T


def pack_units(a, L):
    def tiles(w):
        return w.reshape(KT, P, -1, P).transpose(2, 1, 0, 3).reshape(-1, P, KT * P)

    w_in = a["w_in"][L]
    hy = w_in[:, 1568:]
    gate, up = tiles(a["w_gate"][L]), tiles(a["w_up"][L])
    return np.concatenate([
        tiles(w_in[:, :1024]), tiles(hy), tiles(w_in[:, 1024:1536]), tiles(a["w_out"][L]),
        np.stack([gate, up], axis=1).reshape(-1, P, KT * P), a["w_down"][L].reshape(FT, P, D_MODEL),
    ])


def pack_par(a, L):
    par = np.zeros((P, N_PAR), np.float32)
    par[:, C_GLR:C_NMIX] = a["w_in"][L][:, 1536:1568].reshape(KT, P, 2 * RANK).transpose(1, 0, 2).reshape(P, -1)
    par[:, C_NMIX:C_NFFN] = columns(a["norm_mix"][L])
    par[:, C_NFFN:C_CW] = columns(a["norm_ffn"][L])
    for tap in range(3):
        par[:, C_CW + 12 * tap:C_CW + 12 * tap + 12] = columns(a["hy_conv_w"][L][tap])
    par[:, C_CB:C_GN] = columns(a["hy_conv_b"][L])
    par[:, C_GN] = a["gla_norm"][L]
    for h in range(HEADS):
        k = slice(DK * h, DK * h + DK)
        par[0:DK, C_BG + h] = a["gla_bg_f"][L][k]
        par[DK:P, C_BG + h] = a["gla_bg_b"][L][k]
        par[0:RANK, C_MISC + P * h:C_MISC + P * h + DK] = a["gla_wg_f"][L][:, k]
        par[RANK:2 * RANK, C_MISC + P * h + DK:C_MISC + P * h + P] = a["gla_wg_b"][L][:, k]
    par[:, C_HN:C_B1] = columns(a["hy_norm"][L])
    par[0:FFN_HY, C_B1] = a["hy_b1"][L]
    par[0:FFN_HY, C_F1] = a["hy_freq1"][L]
    for d in range(2):
        rows = slice(FFN_HY * d, FFN_HY * (d + 1))
        par[rows, C_B2] = a["hy_b2"][L]
        par[rows, C_F2] = a["hy_freq2"][L]
        par[0:FFN_HY, C_W2 + FFN_HY * d:C_W2 + FFN_HY * (d + 1)] = a["hy_w2"][L]
        par[rows, C_W3:N_PAR] = a["hy_w3"][L].reshape(FFN_HY, ORDERS, 2, HY)[:, :, d].reshape(FFN_HY, -1)
    par[0:EMB, C_W1:C_W1 + FFN_HY] = a["hy_w1"][L]
    par[SKIP_ROW, C_MISC:C_W3] = a["hy_skip"][L].reshape(-1)
    return par


def kernel(**inputs):
    import concourse.bacc as bacc
    from concourse.bass_utils import run_bass_kernel_spmd

    a = {k: np.asarray(v) for k, v in inputs.items()}
    xs = np.concatenate([a["x_prompt"].reshape(SEQ, D_MODEL), a["x_sample"].reshape(SEQ, D_MODEL)])
    cst, masks = constants()
    arrays = {
        "in_x": np.ascontiguousarray(xs.T.reshape(KT, P, TOK).transpose(1, 0, 2).reshape(P, -1)),
        "in_units": np.ascontiguousarray(np.concatenate([pack_units(a, L) for L in range(DEPTH)])),
        "in_par": np.stack([pack_par(a, L) for L in range(DEPTH)]),
        "in_cst": cst,
        "in_mask": masks,
        "in_fin": np.ascontiguousarray(columns(a["norm_final"])),
    }
    nc = bacc.Bacc("TRN2", target_bir_lowering=False, num_devices=1, dynamic_dma_scratch_size=1024)
    args = [nc.dram_tensor(n, v.shape, mybir.dt.from_np(v.dtype), kind="ExternalInput").ap()
            for n, v in arrays.items()]
    y = nc.dram_tensor("out_y", (P, KT, TOK), F32, kind="ExternalOutput").ap()
    build(nc, *args, y)
    r = run_bass_kernel_spmd(nc, [arrays], core_ids=[0])
    y = r.results[0]["out_y"].transpose(2, 1, 0).reshape(NSEQ, 1, SEQ, D_MODEL)
    return np.ascontiguousarray(y[0]), np.ascontiguousarray(y[1])
```
